# Optimizing a Trainium2 kernel written in Bass

```python
import math
import jax, jax.numpy as jnp
from jax import lax
import numpy as np

D_MODEL = 2048
BATCH = 1
SEQ = 256
DEPTH = 1

CHUNK = 64
WINDOW = 128
WIN_CHUNKS = WINDOW // CHUNK
BAND = WIN_CHUNKS * CHUNK
ATT_HEAD_DIM = 64
ATT_HEADS = D_MODEL // ATT_HEAD_DIM
ATT_GQA_RATIO = 8
ATT_KV_HEADS = ATT_HEADS // ATT_GQA_RATIO
ATT_GROUP = ATT_HEADS // ATT_KV_HEADS
ATT_WIDTH = ATT_HEADS * ATT_HEAD_DIM
ATT_KV_WIDTH = ATT_KV_HEADS * ATT_HEAD_DIM
RET_HEADS = 8
RET_V_DIM = D_MODEL // RET_HEADS
RET_QK_DIM = RET_V_DIM // 2
RET_QK_WIDTH = RET_HEADS * RET_QK_DIM
RET_V_WIDTH = RET_HEADS * RET_V_DIM
IN_SPLITS = (ATT_WIDTH, ATT_KV_WIDTH, ATT_KV_WIDTH, ATT_WIDTH,
             RET_QK_WIDTH, RET_QK_WIDTH, RET_V_WIDTH, RET_V_WIDTH,
             D_MODEL, D_MODEL)
IN_COLS = sum(IN_SPLITS)
EPS = 1e-6
NEG_INF = -1e30

kernel_name = "hybrid_swa_sink_retention_gated_block"

def _rmsnorm(x, w):
    xf = x.astype(jnp.float32)
    y = xf * lax.rsqrt(jnp.mean(xf * xf, axis=-1, keepdims=True) + EPS)
    return (y * w.astype(jnp.float32)).astype(x.dtype)

def _alibi_slopes(n_heads):
    return jnp.exp2(-8.0 * jnp.arange(1, n_heads + 1, dtype=jnp.float32) / n_heads)

def _split_cols(u):
    offs = np.cumsum(IN_SPLITS)[:-1].tolist()
    return jnp.split(u, offs, axis=-1)

def _window_attention(q, k, v, q_norm_w, k_norm_w, sinks):
    b, s, _ = q.shape
    nc = s // CHUNK
    q = q.reshape(b, nc, CHUNK, ATT_KV_HEADS, ATT_GROUP, ATT_HEAD_DIM)
    k = k.reshape(b, nc, CHUNK, ATT_KV_HEADS, ATT_HEAD_DIM)
    v = v.reshape(b, nc, CHUNK, ATT_KV_HEADS, ATT_HEAD_DIM)
    q = _rmsnorm(q, q_norm_w)
    k = _rmsnorm(k, k_norm_w)
    pad = WIN_CHUNKS - 1
    pw = ((0, 0), (pad, 0), (0, 0), (0, 0), (0, 0))
    kp, vp = jnp.pad(k, pw), jnp.pad(v, pw)
    kb = jnp.concatenate([kp[:, w:w + nc] for w in range(WIN_CHUNKS)], axis=2)
    vb = jnp.concatenate([vp[:, w:w + nc] for w in range(WIN_CHUNKS)], axis=2)
    scale = 1.0 / math.sqrt(ATT_HEAD_DIM)
    scores = jnp.einsum('bcqhgd,bckhd->bchgqk', q, kb).astype(jnp.float32) * scale
    qpos = jnp.arange(CHUNK) + pad * CHUNK
    kpos = jnp.arange(BAND)
    dist = jnp.abs(qpos[:, None] - kpos[None, :]).astype(jnp.float32)
    slopes = _alibi_slopes(ATT_HEADS).reshape(ATT_KV_HEADS, ATT_GROUP, 1, 1)
    scores = scores - slopes * dist
    key_chunk = jnp.arange(nc)[:, None] - pad + (kpos // CHUNK)[None, :]
    valid = (key_chunk >= 0)[None, :, None, None, None, :]
    scores = jnp.where(valid, scores, NEG_INF)
    sink = sinks.astype(jnp.float32).reshape(ATT_KV_HEADS, ATT_GROUP, 1, 1)
    m = jnp.maximum(jnp.max(scores, axis=-1, keepdims=True), sink)
    p = jnp.exp(scores - m)
    denom = jnp.sum(p, axis=-1, keepdims=True) + jnp.exp(sink - m)
    probs = (p / denom).astype(v.dtype)
    o = jnp.einsum('bchgqk,bckhd->bcqhgd', probs, vb)
    return o.reshape(b, s, ATT_WIDTH)

def _retention(q, k, v, gn_w):
    b, s, _ = q.shape
    nc = s // CHUNK
    q = q.astype(jnp.float32).reshape(b, nc, CHUNK, RET_HEADS, RET_QK_DIM)
    k = k.astype(jnp.float32).reshape(b, nc, CHUNK, RET_HEADS, RET_QK_DIM) * (RET_QK_DIM ** -0.5)
    v = v.astype(jnp.float32).reshape(b, nc, CHUNK, RET_HEADS, RET_V_DIM)
    log_g = jnp.log(1.0 - jnp.exp2(-5.0 - jnp.arange(RET_HEADS, dtype=jnp.float32)))
    idx = jnp.arange(CHUNK, dtype=jnp.float32)
    d_intra = jnp.exp(jnp.abs(idx[:, None] - idx[None, :])[None] * log_g[:, None, None])
    att = jnp.einsum('bcihd,bcjhd->bchij', q, k) * d_intra
    o_intra = jnp.einsum('bchij,bcjhe->bcihe', att, v)
    zeta = jnp.exp((CHUNK - 1 - idx)[None, :] * log_g[:, None])
    xi = jnp.exp((idx + 1.0)[None, :] * log_g[:, None])
    g_chunk = jnp.exp(CHUNK * log_g)[None, :, None, None]
    upd = jnp.einsum('bcjhd,bcjhe,hj->bchde', k, v, zeta)

    def step(state, u):
        return g_chunk * state + u, state

    s0 = jnp.zeros((b, RET_HEADS, RET_QK_DIM, RET_V_DIM), jnp.float32)
    _, states = lax.scan(step, s0, jnp.moveaxis(upd, 1, 0))
    states = jnp.moveaxis(states, 0, 1)
    o_inter = jnp.einsum('bcihd,bchde,hi->bcihe', q, states, xi)
    o = (o_intra + o_inter).reshape(b, s, RET_HEADS, RET_V_DIM)
    mu = jnp.mean(o, axis=-1, keepdims=True)
    var = jnp.mean(jnp.square(o - mu), axis=-1, keepdims=True)
    o = (o - mu) * lax.rsqrt(var + EPS)
    return o.reshape(b, s, RET_V_WIDTH) * gn_w.astype(jnp.float32)

def setup_inputs(seed: int = 0) -> dict:
    key = jax.random.key(seed)
    ks = jax.random.split(key, 10)
    f32 = jnp.float32
    x = jax.random.normal(ks[0], (BATCH, SEQ, D_MODEL), f32)
    norm_w = 1.0 + 0.02 * jax.random.normal(ks[1], (DEPTH, D_MODEL), f32)
    w_in = jax.random.normal(ks[2], (DEPTH, D_MODEL, IN_COLS), f32) * D_MODEL ** -0.5
    q_norm_w = 1.0 + 0.02 * jax.random.normal(ks[3], (DEPTH, ATT_HEAD_DIM), f32)
    k_norm_w = 1.0 + 0.02 * jax.random.normal(ks[4], (DEPTH, ATT_HEAD_DIM), f32)
    sinks = 0.5 * jax.random.normal(ks[5], (DEPTH, ATT_HEADS), f32)
    ret_gn_w = 1.0 + 0.02 * jax.random.normal(ks[6], (DEPTH, RET_V_WIDTH), f32)
    w_br_attn = jax.random.normal(ks[7], (DEPTH, ATT_WIDTH, D_MODEL), f32) * ATT_WIDTH ** -0.5
    w_br_ret = jax.random.normal(ks[8], (DEPTH, RET_V_WIDTH, D_MODEL), f32) * RET_V_WIDTH ** -0.5
    w_out = jax.random.normal(ks[9], (DEPTH, D_MODEL, D_MODEL), f32) * D_MODEL ** -0.5
    return {"x": x, "norm_w": norm_w, "w_in": w_in, "q_norm_w": q_norm_w, "k_norm_w": k_norm_w,
            "sinks": sinks, "ret_gn_w": ret_gn_w, "w_br_attn": w_br_attn, "w_br_ret": w_br_ret,
            "w_out": w_out}

def reference(x, norm_w, w_in, q_norm_w, k_norm_w, sinks, ret_gn_w, w_br_attn, w_br_ret, w_out):
    for layer in range(DEPTH):
        h = _rmsnorm(x, norm_w[layer])
        u = jnp.einsum('bsd,dn->bsn', h, w_in[layer])
        aq, ak, av, az, rq, rk, rv, rz, ga, gr = _split_cols(u)
        o_a = _window_attention(aq, ak, av, q_norm_w[layer], k_norm_w[layer], sinks[layer])
        o_r = _retention(rq, rk, rv, ret_gn_w[layer])
        y_a = jnp.einsum('bsn,nd->bsd', (o_a * jax.nn.silu(az)).astype(x.dtype), w_br_attn[layer])
        y_r = jnp.einsum('bsn,nd->bsd', (o_r * jax.nn.silu(rz)).astype(x.dtype), w_br_ret[layer])
        merged = jax.nn.sigmoid(ga) * y_a + jax.nn.sigmoid(gr) * y_r
        x = x + jnp.einsum('bsd,de->bse', merged, w_out[layer]).astype(x.dtype)
    return x


_drawn_inputs = setup_inputs


def setup_inputs(seed=0):
    import zlib

    import numpy as np

    out = dict(_drawn_inputs(seed))
    spreads = {}
    factors = {'norm_w': 4.142, 'q_norm_w': 8.0, 'k_norm_w': 8.0, 'sinks': 8.0, 'ret_gn_w': 8.0}
    for name, (base, spread) in spreads.items():
        noise = np.random.default_rng([zlib.crc32(name.encode()), seed]).standard_normal(out[name].shape)
        drawn = base * np.exp(spread * noise) if base else spread * noise
        out[name] = __import__('jax').numpy.asarray(drawn.astype(out[name].dtype))
    for name, factor in factors.items():
        out[name] = (out[name] * factor).astype(out[name].dtype)
    return out
```

```python
from contextlib import ExitStack

import concourse.bass as bass
from concourse import mybir

P = 128
SEQ = 256
D = 2048
CHUNK = 64
HD = 64
HEADS = D // HD
KV_HEADS = 4
GROUP = HEADS // KV_HEADS
KVW = KV_HEADS * HD
RET_HEADS = 8
RET_QK = 128
RET_V = D // RET_HEADS
EPS = 1e-6

TOK = SEQ // P
KT = D // P
NB = 512
CPB = 8
KPC = KT // CPB
RING = 4
CT = NB // P

COL_AQ, COL_KV = 0, D
COL_AZ = COL_KV + 2 * KVW
COL_RQK = COL_AZ + D
COL_RV = COL_RQK + 2 * RET_HEADS * RET_QK
COL_RZ = COL_RV + D
COL_GA = COL_RZ + D
COL_GR = COL_GA + D

B_KV, B_Q, B_MIX, B_BRA, B_GA, B_GR0, B_MERGE, B_BR3, B_OUT, B_END = 0, 1, 5, 21, 25, 29, 30, 36, 37, 41
MIX_TURNS, MIX_BLOCKS = 4, 4
RET_TURNS, RET_PER = 2, 4
MERGE_TURNS = 3
FIRST_SPLITS = ((0,), (1, 2), (3,), ())

ALU = mybir.AluOpType
ACT = mybir.ActivationFunctionType
AX_X = mybir.AxisListType.X
F32 = mybir.dt.float32
F32R = mybir.dt.float32r


class Blk:

    def __init__(self, const, per_turn=0, turn=None):
        self.const, self.per_turn, self.turn = const, per_turn, turn

    def __add__(self, n):
        return Blk(self.const + n, self.per_turn, self.turn)

    def _value(self, factor, const):
        return const if self.turn is None else self.turn * (self.per_turn * factor) + const

    def chunks(self, c):
        return self._value(CPB, CPB * self.const + c)

    def loads(self, c):
        per_block = CPB // RING
        return self._value(16 * per_block, 16 * (per_block * self.const + c // RING + 1))

    def evacuated_before(self):
        assert self.per_turn % 2 == 0
        n = self.const // 2 + 1
        return n if self.turn is None else self.turn * (self.per_turn // 2) + n

    def evacuated(self):
        return self.evacuated_before() + 1

    @property
    def parity(self):
        return self.const % 2

    def reuses_slot(self, c):
        return self.turn is not None or CPB * self.const + c >= RING


class StepCount:

    def __init__(self, sem):
        self.sem, self.n, self.turn = sem, 0, None

    def enter(self, turn, per_turn):
        self.turn, self.per_turn, self.start = turn, per_turn, self.n

    def leave(self, turns):
        assert self.n - self.start == self.per_turn, (self.n - self.start, self.per_turn)
        self.n, self.turn = self.start + self.per_turn * turns, None

    def mark(self, instruction):
        instruction.then_inc(self.sem, 1)
        self.n += 1

    def value(self):
        return self.n if self.turn is None else self.turn * self.per_turn + self.n


def hybrid_block_kernel(nc, x, norm_w, w_in, q_norm_w, k_norm_w, sinks, ret_gn_w,
                        w_br_attn, w_br_ret, w_out, identity, distance, neg_slopes, decay, out):
    x_v = x.rearrange("b (t p) d -> p (b t) d", p=P)
    out_v = out.rearrange("b (t p) d -> p (b t) d", p=P)

    def weight_view(w):
        return w.rearrange("l (k p) n -> p (l k) n", p=P)

    w_in_v, w_bra_v, w_brr_v, w_out_v = (weight_view(w) for w in (w_in, w_br_attn, w_br_ret, w_out))

    with ExitStack() as ctx:
        at = [(nc.sbuf_base + 31) // 32 * 32]

        def region(size):
            start = at[0]
            at[0] += size
            return start

        def sb(name, shape, offset, dt=F32):
            size = 4
            for n in shape[1:]:
                size *= n
            end = (offset + size + 31) // 32 * 32
            return nc.alloc_sbuf_tensor_at(name, shape, dt, offset=offset), end

        KB = 1024
        r_h = region(32 * KB)
        r_ring = region(48 * KB)
        r_g = region(32 * KB)
        r_q = region(16 * KB)
        r_qk = region(16 * KB)
        r_rv = region(16 * KB)
        r_rz = region(16 * KB)
        r_ya = region(16 * KB)
        r_stage = region(12 * KB)
        r_small = region(0)

        hT_hi, o = sb("hT_hi", [P, KT, SEQ], r_h, F32R)
        hT_lo, o = sb("hT_lo", [P, KT, SEQ], o, F32R)
        w_raw, o = sb("w_raw", [P, RING, KPC, NB], r_ring)
        w_hi, o = sb("w_hi", [P, RING, KPC, NB], o, F32R)
        w_lo, o = sb("w_lo", [P, RING, KPC, NB], o, F32R)
        gT_hi, o = sb("gT_hi", [P, KT, SEQ], r_g, F32R)
        gT_lo, o = sb("gT_lo", [P, KT, SEQ], o, F32R)

        q, _ = sb("q", [P, TOK, D], r_q)
        decay_s, o = sb("decay_s", [P, RET_HEADS, SEQ], r_q)
        kstage, o = sb("kstage", [P, RET_PER, SEQ], o)
        ret_w, _ = sb("ret_w", [P, 2, 384], o)

        rqkT, _ = sb("rqkT", [P, 2 * RET_HEADS, SEQ], r_qk)
        rv, _ = sb("rv", [P, TOK, D], r_rv)
        x_s, _ = sb("x_s", [P, TOK, D], r_rv)
        mT_hi, _ = sb("mT_hi", [P, KT, SEQ], r_qk, F32R)
        mT_lo, _ = sb("mT_lo", [P, KT, SEQ], r_rv, F32R)
        rz, _ = sb("rz", [P, TOK, D], r_rz)
        squares, _ = sb("squares", [P, TOK, D], r_rz)
        res, _ = sb("res", [P, TOK, D], r_rz)

        y, _ = sb("y", [P, TOK, D], r_ya)
        kv, o = sb("kv", [P, TOK, NB], r_ya)
        v_low, o = sb("v_low", [HD, KVW], o)
        kdup, o = sb("kdup", [P, TOK, 2, HD], o)
        kT, o = sb("kT", [P, SEQ], o)
        scores, o = sb("scores", [P, 2, 320], o)
        probs, o = sb("probs", [P, 2, 320], o)
        pT, o = sb("pT", [P, 2, 384], o)
        vec_rows, o = sb("vec_rows", [34, P], o)
        slopes_s, o = sb("slopes_s", [P, HEADS], o)
        sinks_s, o = sb("sinks_s", [P, HEADS], o)
        neg_sinks, o = sb("neg_sinks", [P, HEADS], o)
        assert o <= r_stage

        gate, o = sb("gate", [P, TOK, NB], r_stage)
        qstage, o2 = sb("qstage", [P, TOK, NB], o)
        rqk_stage, _ = sb("rqk_stage", [P, TOK, NB], o)
        qT, _ = sb("qT", [P, CT, SEQ], o2)
        ret_gated, _ = sb("ret_gated", [P, TOK, RET_PER * RET_V], o)
        merged, _ = sb("merged", [P, TOK, NB], o)

        ident, o = sb("ident", [P, P], r_small)
        dist_s, o = sb("dist_s", [P, 320], o)
        cols, o = sb("cols", [P, 34], o)
        ssq, o = sb("ssq", [P, 2], o)
        rstd_x, o = sb("rstd_x", [P, 2], o)
        qk_ss, o = sb("qk_ss", [P, TOK, 36], o)
        rstd_qk, o = sb("rstd_qk", [P, TOK, 36], o)
        root, o = sb("root", [P, 72], o)
        newton, o = sb("newton", [P, 72], o)
        neg_max, o = sb("neg_max", [P, GROUP, 2], o)
        row_max, o = sb("row_max", [P, 2, 2], o)
        denom, o = sb("denom", [P, 2, GROUP], o)
        sink_p, o = sb("sink_p", [P, 2, GROUP], o)
        bn, o = sb("bn", [P, 2, 2, 6], o)
        moments, o = sb("moments", [P, RET_PER, 2, 2], o)
        var_ret, o = sb("var_ret", [P, RET_PER * 2], o)
        rstd_ret, o = sb("rstd_ret", [P, RET_PER * 2], o)
        filler, o = sb("filler", [P, 1], o)
        assert o <= nc.sbuf_usable_end, (o, nc.sbuf_usable_end)

        acc = [[ctx.enter_context(nc.psum_tensor(f"acc{p}{t}", [P, NB], F32)) for t in range(TOK)]
               for p in range(2)]
        mis = [ctx.enter_context(nc.psum_tensor(f"mis{m}", [P, NB], F32)) for m in range(4)]

        def sem(name):
            return ctx.enter_context(nc.semaphore(name))

        raw_loaded = [sem(f"raw_loaded{s}") for s in range(RING)]
        hi_ready, lo_ready, chunk_used = sem("hi_ready"), sem("lo_ready"), sem("chunk_used")
        acc_free = [sem("acc_free0"), sem("acc_free1")]
        gate_ready = sem("gate_ready")
        x_loaded = [sem(f"x_loaded{g}") for g in range(4)]
        consts_loaded, ident_loaded = sem("consts_loaded"), sem("ident_loaded")
        cols_T, cols_ready = sem("cols_T"), sem("cols_ready")
        xT_done, hT_hi_ready, hT_ready = sem("xT_done"), sem("hT_hi_ready"), sem("hT_ready")
        ssq_ready, var_ready, root_ready = sem("ssq_ready"), sem("var_ready"), sem("root_ready")
        dve_step = sem("dve_step")
        kv_ready, v_low_loaded = sem("kv_ready"), sem("v_low_loaded")
        qk_staged, qkT_done, qkT_ready = sem("qk_staged"), sem("qkT_done"), sem("qkT_ready")
        scores_done, neg_max_ready, probs_ready = sem("scores_done"), sem("neg_max_ready"), sem("probs_ready")
        pT_done, pT_ready, pv_done = sem("pT_done"), sem("pT_ready"), sem("pv_done")
        sink_sum_ready, sink_exp_ready = sem("sink_sum_ready"), sem("sink_exp_ready")
        gated_ready, gT_done, gT_hi_ready, gT_ready = sem("gated_ready"), sem("gT_done"), sem("gT_hi_ready"), sem("gT_ready")
        rqkT_done, rqkT_ready = sem("rqkT_done"), sem("rqkT_ready")
        decay_loaded, keys_copied = sem("decay_loaded"), sem("keys_copied")
        ret_scores, ret_weighted, ret_done = sem("ret_scores"), sem("ret_weighted"), sem("ret_done")
        ret_centred = sem("ret_centred")
        ret_staged, retT_done = sem("ret_staged"), sem("retT_done")
        y_scaled = sem("y_scaled")
        merged_ready, mT_done, mT_hi_ready, mT_ready = sem("merged_ready"), sem("mT_done"), sem("mT_hi_ready"), sem("mT_ready")
        res_loaded, out_ready, out_stored = sem("res_loaded"), sem("out_ready"), sem("out_stored")

        N_CONSTS = 9
        block = ctx.enter_context(nc.Block())

        @block.sync
        def _(sp):
            def load_chunk(b, c, view, col):
                if b.reuses_slot(c):
                    sp.wait_ge(lo_ready, b.chunks(c) - RING + 1)
                sp.dma_start(w_raw[:, c % RING], view[:, KPC * c:KPC * (c + 1), bass.ds(col, NB)]
                             ).then_inc(raw_loaded[c % RING], 16)

            def load_block(b, view, col):
                for c in range(CPB):
                    load_chunk(b, c, view, col)

            for c in range(CPB):
                if c < 4:
                    sp.dma_start(x_s[:, :, c * NB:(c + 1) * NB], x_v[:, :, c * NB:(c + 1) * NB]
                                 ).then_inc(x_loaded[c], 16)
                load_chunk(Blk(B_KV), c, w_in_v, COL_KV)
            with sp.Fori(0, 4) as i:
                load_block(Blk(B_Q, 1, i), w_in_v, COL_AQ + NB * i)
            with sp.Fori(0, MIX_TURNS) as i:
                for k, col in enumerate((COL_RQK, COL_AZ, COL_RV, COL_RZ)):
                    load_block(Blk(B_MIX + k, MIX_BLOCKS, i), w_in_v, col + NB * i)
            with sp.Fori(0, 4) as i:
                load_block(Blk(B_BRA, 1, i), w_bra_v, NB * i)
            with sp.Fori(0, 4) as i:
                load_block(Blk(B_GA, 1, i), w_in_v, COL_GA + NB * i)
            load_block(Blk(B_GR0), w_in_v, COL_GR)
            with sp.Fori(0, MERGE_TURNS) as i:
                load_block(Blk(B_MERGE, 2, i), w_brr_v, NB * i)
                load_block(Blk(B_MERGE + 1, 2, i), w_in_v, COL_GR + NB + NB * i)
            load_block(Blk(B_BR3), w_brr_v, 3 * NB)
            with sp.Fori(0, 4) as i:
                load_block(Blk(B_OUT, 1, i), w_out_v, NB * i)
            for f in range(4):
                for t in range(TOK):
                    sp.wait_ge(out_ready, TOK * f + t + 1)
                    sp.dma_start(out_v[:, t, f * NB:(f + 1) * NB], res[:, t, f * NB:(f + 1) * NB]
                                 ).then_inc(out_stored, 16)
            sp.wait_ge(out_stored, 16 * 4 * TOK)

        @block.gpsimd
        def _(pool):
            pool.wait_ge(acc_free[0], Blk(B_KV).evacuated())
            pool.dma_start(v_low[:, :], kv[HD:P, 0, KVW:2 * KVW]).then_inc(v_low_loaded, 16)
            pool.wait_ge(qk_staged, MIX_TURNS)
            pool.dma_start(decay_s[:, :, :], decay).then_inc(decay_loaded, 16)
            pool.wait_ge(ret_staged, RET_TURNS)
            pool.dma_start(res[:, :, :], x_v).then_inc(res_loaded, 16)

        @block.scalar
        def _(act):
            def split_at(first, place):
                b, c = first + place // CPB, place % CPB
                act.wait_ge(raw_loaded[c % RING], b.loads(c))
                if b.reuses_slot(c):
                    act.wait_ge(chunk_used, b.chunks(c) - RING + 1)
                nc.scalar.activation(w_hi[:, c % RING], w_raw[:, c % RING], ACT.Copy).then_inc(hi_ready, 1)

            def sigmoid_of(b, dst, merge_gate):
                act.wait_ge(chunk_used, b.chunks(CPB))
                for t in range(TOK):
                    ins = nc.scalar.activation(dst(t), acc[b.parity][t][:, :], ACT.Sigmoid,
                                               scale=rstd_x[:, t:t + 1])
                    if not merge_gate:
                        ins.then_inc(gate_ready, 1)
                if merge_gate:
                    ins.then_inc(acc_free[b.parity], 1)

            def root_of(n, v):
                act.wait_ge(var_ready, n)
                nc.scalar.activation(root[:, 0:v.shape[-1]], v, ACT.Sqrt).then_inc(root_ready, 1)

            act.dma_start(ident[:, :], identity).then_inc(ident_loaded, 16)
            act.dma_start(vec_rows[0:16, :], norm_w.rearrange("l (k p) -> (l k) p", p=P)).then_inc(consts_loaded, 16)
            act.dma_start(vec_rows[16:32, :], ret_gn_w.rearrange("l (k p) -> (l k) p", p=P)).then_inc(consts_loaded, 16)
            for k in range(2):
                act.dma_start(vec_rows[32:33, k * HD:(k + 1) * HD], q_norm_w).then_inc(consts_loaded, 16)
                act.dma_start(vec_rows[33:34, k * HD:(k + 1) * HD], k_norm_w).then_inc(consts_loaded, 16)
            act.dma_start(dist_s[:, :], distance).then_inc(consts_loaded, 16)
            act.dma_start(slopes_s[:, :], neg_slopes.broadcast_to([P, HEADS])).then_inc(consts_loaded, 16)
            act.dma_start(sinks_s[:, :], sinks.broadcast_to([P, HEADS])).then_inc(consts_loaded, 16)

            act.wait_ge(cols_ready, 1)
            for g in range(4):
                for m in (2 * g, 2 * g + 1):
                    act.wait_ge(xT_done, m + 1)
                    for e in range(2):
                        ins = nc.scalar.activation(hT_hi[:, 2 * m + e, :], mis[m % 4][:, e * SEQ:(e + 1) * SEQ],
                                                   ACT.Copy, scale=cols[:, 2 * m + e:2 * m + e + 1])
                    ins.then_inc(hT_hi_ready, 1)
                for c in FIRST_SPLITS[g]:
                    split_at(Blk(B_KV), c)
            for t in range(TOK):
                nc.scalar.activation(squares[:, t, :], x_s[:, t, :], ACT.Square,
                                     accum_out=ssq[:, t:t + 1]).then_inc(ssq_ready, 1)
            root_of(1, ssq[:, :])
            for place in range(4, 12):
                split_at(Blk(B_KV), place)
            with act.Fori(0, 2) as i:
                for place in range(4, 20):
                    split_at(Blk(B_Q, 2, i), place)
            root_of(2, qk_ss.rearrange("p t h -> p (t h)"))

            with act.Fori(0, MIX_TURNS) as i:
                b = Blk(B_MIX, MIX_BLOCKS, i)
                for place in range(4, 36):
                    split_at(b, place)
                    if place % 2 == 0 and 0 <= (place - 8) // 2 < GROUP:
                        h = (place - 8) // 2
                        act.wait_ge(neg_max_ready, GROUP * i + h + 1)
                        nc.scalar.activation(probs[:, h % 2, 0:128], scores[:, h % 2, 0:128], ACT.Exp,
                                             bias=neg_max[:, h, 0:1], accum_out=denom[:, 0, h:h + 1])
                        nc.scalar.activation(probs[:, h % 2, 128:320], scores[:, h % 2, 128:320], ACT.Exp,
                                             bias=neg_max[:, h, 1:2], accum_out=denom[:, 1, h:h + 1]
                                             ).then_inc(probs_ready, 1)
                    if place == 19:
                        sigmoid_of(b + 1, lambda t: gate[:, t, :], merge_gate=False)
                    if place == 24:
                        act.wait_ge(sink_sum_ready, i + 1)
                        nc.scalar.activation(sink_p[:, :, :], sink_p[:, :, :], ACT.Exp).then_inc(sink_exp_ready, 1)
                    if place == 30:
                        act.wait_ge(gT_done, i + 1)
                        for m in range(2):
                            nc.scalar.activation(
                                gT_hi[:, bass.ds(4 * i + 2 * m, 2), :],
                                mis[2 + m].rearrange("p (c s) -> p c s", c=2), ACT.Copy).then_inc(gT_hi_ready, 1)
                    if place == 35:
                        sigmoid_of(b + 3, lambda t: rz[:, t, bass.ds(NB * i, NB)], merge_gate=False)

            with act.Fori(0, 2) as i:
                for place in range(4, 20):
                    split_at(Blk(B_BRA, 2, i), place)

            act.wait_ge(rqkT_ready, MIX_TURNS)
            with act.Fori(0, RET_TURNS) as j:
                b = Blk(B_GA, 2, j)
                for place in range(4, 20):
                    split_at(b, place)
                    if place == 4:
                        nc.scalar.activation(kstage[:, :, :], rqkT[:, bass.ds(RET_PER * j + RET_HEADS, RET_PER), :],
                                             ACT.Copy).then_inc(keys_copied, 1)
                    if place in (11, 19):
                        e = place // 19
                        act.wait_ge(y_scaled, 2 * j + (e + 1))
                        sigmoid_of(b + e, lambda t: gate[:, t, :], merge_gate=True)
                    if place == 15:
                        root_of(3 + j, var_ret[:, :])
                    if place == 19:
                        act.wait_ge(retT_done, j + 1)
                        for c in range(8):
                            ins = nc.scalar.activation(
                                gT_hi[:, bass.ds(8 * j + c, 1), :],
                                mis[c // 2][:, (c % 2) * SEQ:(c % 2 + 1) * SEQ].unsqueeze(1), ACT.Copy,
                                scale=cols[:, bass.ds(8 * j + (KT + c), 1)])
                            if c % 2:
                                ins.then_inc(gT_hi_ready, 1)

            def split_merged(i):
                act.wait_ge(mT_done, i + 1)
                for m in range(2):
                    nc.scalar.activation(mT_hi[:, bass.ds(4 * i + 2 * m, 2), :],
                                         mis[m].rearrange("p (c s) -> p c s", c=2), ACT.Copy
                                         ).then_inc(mT_hi_ready, 1)

            for place in range(4, 12):
                split_at(Blk(B_GR0), place)
            act.wait_ge(y_scaled, 4 + 1)
            sigmoid_of(Blk(B_GR0), lambda t: gate[:, t, :], merge_gate=True)
            with act.Fori(0, MERGE_TURNS) as i:
                b = Blk(B_MERGE, 2, i)
                for place in range(4, 20):
                    split_at(b, place)
                    if place == 14:
                        split_merged(i)
                    if place == 19:
                        act.wait_ge(merged_ready, i + 1)
                        sigmoid_of(b + 1, lambda t: gate[:, t, :], merge_gate=True)
            for place in range(4, CPB * (B_END - B_BR3)):
                split_at(Blk(B_BR3), place)
                if place == 14:
                    split_merged(MERGE_TURNS)

        @block.vector
        def _(dve):
            own = StepCount(dve_step)

            def step(ins):
                own.mark(ins)
                dve.wait_ge(dve_step, own.value())

            def split_at(first, place):
                b, c = first + place // CPB, place % CPB
                dve.wait_ge(hi_ready, b.chunks(c + 1))
                nc.vector.tensor_tensor(w_lo[:, c % RING], w_raw[:, c % RING], w_hi[:, c % RING].bitcast(F32),
                                        ALU.subtract).then_inc(lo_ready, 1)

            def rsqrt(n, v, y):
                w = v.shape[-1]
                t = newton[:, 0:w]
                dve.wait_ge(root_ready, n)
                step(nc.vector.reciprocal(y, root[:, 0:w]))
                step(nc.vector.tensor_tensor(t, y, y, ALU.mult))
                step(nc.vector.tensor_tensor(t, t, v, ALU.mult))
                step(nc.vector.tensor_scalar(t, t, -0.5, 1.5, ALU.mult, ALU.add))
                step(nc.vector.tensor_tensor(y, y, t, ALU.mult))

            def scaled(b, dst):
                dve.wait_ge(chunk_used, b.chunks(CPB))
                for t in range(TOK):
                    ins = nc.vector.tensor_scalar(dst(t), acc[b.parity][t][:, :], rstd_x[:, t:t + 1], None, ALU.mult)
                ins.then_inc(acc_free[b.parity], 1)

            def silu_of(b, gates, dst):
                for t in range(TOK):
                    dve.wait_ge(gate_ready, gates + t + 1)
                    ins = nc.vector.scalar_tensor_tensor(dst(t), acc[b.parity][t][:, :], rstd_x[:, t:t + 1],
                                                         dst(t), ALU.mult, ALU.mult)
                ins.then_inc(acc_free[b.parity], 1)

            def squares_of(src, tmp, dst):
                step(nc.vector.tensor_tensor(tmp, src, src, ALU.mult))
                step(nc.vector.tensor_reduce(dst, tmp.rearrange("p (h d) -> p h d", d=HD), AX_X, ALU.add))

            for s in (acc_free[0], acc_free[1], gT_ready, y_scaled):
                dve.sem_inc(s, 1)

            dve.wait_ge(cols_T, 1)
            nc.vector.tensor_copy(cols[:, :], mis[3][:, 0:34]).then_inc(cols_ready, 1)
            dve.wait_ge(cols_ready, 1)
            for g in range(4):
                for m in (2 * g, 2 * g + 1):
                    dve.wait_ge(hT_hi_ready, m + 1)
                    for e in range(2):
                        nc.vector.scalar_tensor_tensor(
                            hT_lo[:, 2 * m + e, :], mis[m % 4][:, e * SEQ:(e + 1) * SEQ],
                            cols[:, 2 * m + e:2 * m + e + 1], hT_hi[:, 2 * m + e, :].bitcast(F32),
                            ALU.mult, ALU.subtract).then_inc(hT_ready, 1)
                for c in FIRST_SPLITS[g]:
                    split_at(Blk(B_KV), c)
            step(nc.vector.tensor_scalar(neg_sinks[:, :], sinks_s[:, :], -1.0, None, ALU.mult))
            dve.wait_ge(ssq_ready, TOK)
            nc.vector.tensor_scalar(ssq[:, :], ssq[:, :], 1.0 / D, EPS, ALU.mult, ALU.add).then_inc(var_ready, 1)
            rsqrt(1, ssq[:, :], rstd_x[:, :])

            for place in range(4, 12):
                split_at(Blk(B_KV), place)
            scaled(Blk(B_KV), lambda t: kv[:, t, :])
            dve.wait_ge(acc_free[0], Blk(B_KV).evacuated())
            for t in range(TOK):
                squares_of(kv[:, t, 0:KVW], gate[:, t, 0:KVW], qk_ss[:, t, HEADS:HEADS + KV_HEADS])

            with dve.Fori(0, 2) as i:
                own.enter(i, 8)
                b = Blk(B_Q, 2, i)
                for place in range(4, 20):
                    split_at(b, place)
                    if place in (11, 19):
                        e = place // 19
                        scaled(b + e, lambda t: q[:, t, bass.ds(2 * NB * i + e * NB, NB)])
                        dve.wait_ge(acc_free[(b + e).parity], (b + e).evacuated())
                        for t in range(TOK):
                            squares_of(q[:, t, bass.ds(2 * NB * i + e * NB, NB)], gate[:, t, :],
                                       qk_ss[:, t, bass.ds(16 * i + 8 * e, 8)])
                own.leave(2)
            all_ss = qk_ss.rearrange("p t h -> p (t h)")
            nc.vector.tensor_scalar(all_ss, all_ss, 1.0 / HD, EPS, ALU.mult, ALU.add).then_inc(var_ready, 1)
            rsqrt(2, all_ss, rstd_qk.rearrange("p t h -> p (t h)"))

            with dve.Fori(0, MIX_TURNS) as i:
                own.enter(i, 2 * GROUP + 3)
                b = Blk(B_MIX, MIX_BLOCKS, i)
                for place in range(4, 36):
                    split_at(b, place)
                    if place == 4:
                        for t in range(TOK):
                            nc.vector.tensor_tensor(
                                qstage[:, t, :].rearrange("p (h d) -> p h d", d=HD),
                                q[:, t, bass.ds(NB * i, NB)].rearrange("p (h d) -> p h d", d=HD),
                                rstd_qk[:, t, bass.ds(GROUP * i, GROUP)].unsqueeze(2).to_broadcast([P, GROUP, HD]),
                                ALU.mult)
                            for e in range(2):
                                ins = nc.vector.tensor_scalar(kdup[:, t, e, :], kv[:, t, bass.ds(HD * i, HD)],
                                                              rstd_qk[:, t, bass.ds(HEADS + i, 1)], None, ALU.mult)
                        ins.then_inc(qk_staged, 1)
                    if place == 6:
                        dve.wait_ge(qkT_done, i + 1)
                        for m in range(2):
                            nc.vector.tensor_scalar(qT[:, 2 * m:2 * m + 2, :].rearrange("p c s -> p (c s)"), mis[m][:, :],
                                                    cols[:, 32:33], HD ** -0.5, ALU.mult, ALU.mult)
                        nc.vector.tensor_scalar(kT[:, :], mis[2][:, 0:SEQ], cols[:, 33:34], None, ALU.mult
                                                ).then_inc(qkT_ready, 1)
                    if place % 2 == 0 and 0 <= (place - 8) // 2 < GROUP:
                        h = (place - 8) // 2
                        head = GROUP * i + h
                        dve.wait_ge(scores_done, head + 1)
                        slope = slopes_s[:, bass.ds(head, 1)]
                        nc.vector.scalar_tensor_tensor(scores[:, h % 2, 0:128], dist_s[:, 0:128], slope,
                                                       mis[0][:, 0:128], ALU.mult, ALU.add)
                        step(nc.vector.scalar_tensor_tensor(scores[:, h % 2, 128:320], dist_s[:, 128:320], slope,
                                                            mis[0][:, 128:320], ALU.mult, ALU.add))
                        nc.vector.tensor_reduce(row_max[:, h % 2, 0:1], scores[:, h % 2, 0:128], AX_X, ALU.max)
                        step(nc.vector.tensor_reduce(row_max[:, h % 2, 1:2], scores[:, h % 2, 128:320], AX_X, ALU.max))
                        nc.vector.scalar_tensor_tensor(neg_max[:, h, :], row_max[:, h % 2, :], -1.0,
                                                       neg_sinks[:, bass.ds(head, 1)].to_broadcast([P, 2]),
                                                       ALU.mult, ALU.min).then_inc(neg_max_ready, 1)
                    if place % 2 == 1 and 0 <= (place - 11) // 2 < GROUP:
                        h = (place - 11) // 2
                        dve.wait_ge(pT_done, GROUP * i + h + 1)
                        nc.vector.tensor_copy(pT[:, h % 2, 0:256], mis[1][:, 0:256])
                        nc.vector.tensor_copy(pT[0:HD, h % 2, 256:384], mis[1][0:HD, 256:384]).then_inc(pT_ready, 1)
                    if place == 11:
                        scaled(b, lambda t: rqk_stage[:, t, :])
                    if place == 19:
                        silu_of(b + 1, 4 * i, lambda t: gate[:, t, :])
                    if place == 24:
                        dve.wait_ge(neg_max_ready, GROUP * i + GROUP)
                        nc.vector.tensor_tensor(
                            sink_p[:, :, :],
                            sinks_s[:, bass.ds(GROUP * i, GROUP)].unsqueeze(1).to_broadcast([P, 2, GROUP]),
                            neg_max.rearrange("p h t -> p t h"), ALU.add).then_inc(sink_sum_ready, 1)
                    if place == 26:
                        dve.wait_ge(probs_ready, GROUP * i + GROUP)
                        dve.wait_ge(sink_exp_ready, i + 1)
                        step(nc.vector.tensor_tensor(denom[:, :, :], denom[:, :, :], sink_p[:, :, :], ALU.add))
                        step(nc.vector.reciprocal(denom[:, :, :], denom[:, :, :]))
                        dve.wait_ge(acc_free[0], (b + 1).evacuated())
                        for t in range(TOK):
                            gate_h = gate[:, t, :].rearrange("p (h d) -> p h d", d=HD)
                            ins = nc.vector.tensor_tensor(
                                gate_h, gate_h, denom[:, t, :].unsqueeze(2).to_broadcast([P, GROUP, HD]), ALU.mult)
                        step(ins)
                    if place == 27:
                        scaled(b + 2, lambda t: rv[:, t, bass.ds(NB * i, NB)])
                    if place == 28:
                        dve.wait_ge(pv_done, i + 1)
                        for t in range(TOK):
                            ins = nc.vector.tensor_tensor(gate[:, t, :], mis[2 + t][:, :], gate[:, t, :], ALU.mult)
                        ins.then_inc(gated_ready, 1)
                    if place == 29:
                        dve.wait_ge(rqkT_done, i + 1)
                        for m in range(2):
                            ins = nc.vector.tensor_copy(rqkT[:, bass.ds(4 * i + 2 * m, 2), :],
                                                        mis[m].rearrange("p (c s) -> p c s", c=2))
                        ins.then_inc(rqkT_ready, 1)
                    if place == 31:
                        for m in range(2):
                            dve.wait_ge(gT_hi_ready, 2 * i + m + 1)
                            ins = nc.vector.tensor_tensor(
                                gT_lo[:, bass.ds(4 * i + 2 * m, 2), :], mis[2 + m].rearrange("p (c s) -> p c s", c=2),
                                gT_hi[:, bass.ds(4 * i + 2 * m, 2), :].bitcast(F32), ALU.subtract)
                        ins.then_inc(gT_ready, 1)
                    if place == 35:
                        silu_of(b + 3, 4 * i + 2, lambda t: rz[:, t, bass.ds(NB * i, NB)])
                own.leave(MIX_TURNS)

            with dve.Fori(0, 2) as i:
                b = Blk(B_BRA, 2, i)
                for place in range(4, 20):
                    split_at(b, place)
                    if place in (11, 19):
                        e = place // 19
                        dve.wait_ge(chunk_used, (b + e).chunks(CPB))
                        for t in range(TOK):
                            ins = nc.vector.tensor_copy(y[:, t, bass.ds(2 * NB * i + e * NB, NB)],
                                                        acc[(b + e).parity][t][:, :])
                        ins.then_inc(acc_free[(b + e).parity], 1)
            for k in (2, 3):
                dve.wait_ge(acc_free[(B_BRA + k) % 2], Blk(B_BRA + k).evacuated())

            dve.wait_ge(decay_loaded, 16)
            with dve.Fori(0, RET_TURNS) as j:
                own.enter(j, 2 * RET_PER + 5)
                b = Blk(B_GA, 2, j)
                for place in range(4, 20):
                    split_at(b, place)
                    if place % 2 == 0 and 0 <= (place - 6) // 2 < RET_PER:
                        n = (place - 6) // 2
                        dve.wait_ge(ret_scores, RET_PER * j + n + 1)
                        head_decay = decay_s[:, bass.ds(RET_PER * j + n, 1), :].rearrange("p a s -> p (a s)")
                        nc.vector.tensor_tensor(ret_w[:, n % 2, 0:SEQ], mis[0][:, 0:SEQ], head_decay, ALU.mult)
                        nc.vector.tensor_tensor(ret_w[:, n % 2, SEQ:SEQ + P], mis[0][:, SEQ:SEQ + P],
                                                head_decay[:, 0:P], ALU.mult).then_inc(ret_weighted, 1)
                    if place % 2 == 0 and 0 <= (place - 8) // 2 < RET_PER:
                        n = (place - 8) // 2
                        dve.wait_ge(ret_done, RET_PER * j + n + 1)
                        o_ps = mis[2 + n % 2]
                        for t in range(TOK):
                            ins = nc.vector.bn_stats(bn[:, n % 2, t, :], o_ps[:, t * RET_V:(t + 1) * RET_V])
                        step(ins)
                        nc.vector.memset(filler[:, :], 0.0)
                        for t in range(TOK):
                            ins = nc.vector.bn_aggr(moments[:, n, t, :], bn[:, n % 2, t, :])
                        step(ins)
                        for t in range(TOK):
                            g = rz[:, t, bass.ds(RET_PER * RET_V * j + RET_V * n, RET_V)]
                            ins = nc.vector.scalar_tensor_tensor(g, o_ps[:, t * RET_V:(t + 1) * RET_V],
                                                                 moments[:, n, t, 0:1], g, ALU.subtract, ALU.mult)
                        ins.then_inc(ret_centred, 1)
                    if place == 15:
                        nc.vector.tensor_scalar(var_ret.rearrange("p (n t) -> p n t", t=2), moments[:, :, :, 1],
                                                EPS, None, ALU.add).then_inc(var_ready, 1)
                    if place == 16:
                        rsqrt(3 + j, var_ret[:, :], rstd_ret[:, :])
                        dve.wait_ge(ret_centred, RET_PER * j + RET_PER)
                        for n in range(RET_PER):
                            for t in range(TOK):
                                ins = nc.vector.tensor_scalar(
                                    ret_gated[:, t, n * RET_V:(n + 1) * RET_V],
                                    rz[:, t, bass.ds(RET_PER * RET_V * j + RET_V * n, RET_V)],
                                    rstd_ret[:, 2 * n + t:2 * n + t + 1], None, ALU.mult)
                        ins.then_inc(ret_staged, 1)
                    if place in (11, 19):
                        e = place // 19
                        dve.wait_ge(acc_free[(b + e).parity], (b + e).evacuated())
                        for t in range(TOK):
                            yb = y[:, t, bass.ds(2 * NB * j + e * NB, NB)]
                            ins = nc.vector.tensor_tensor(yb, yb, gate[:, t, :], ALU.mult)
                        ins.then_inc(y_scaled, 1)
                    if place == 19:
                        for c in range(8):
                            if c % 2 == 0:
                                dve.wait_ge(gT_hi_ready, 4 * j + (8 + c // 2 + 1))
                            ins = nc.vector.scalar_tensor_tensor(
                                gT_lo[:, bass.ds(8 * j + c, 1), :].rearrange("p a s -> p (a s)"),
                                mis[c // 2][:, (c % 2) * SEQ:(c % 2 + 1) * SEQ],
                                cols[:, bass.ds(8 * j + (KT + c), 1)],
                                gT_hi[:, bass.ds(8 * j + c, 1), :].rearrange("p a s -> p (a s)").bitcast(F32),
                                ALU.mult, ALU.subtract)
                        ins.then_inc(gT_ready, 1)
                own.leave(RET_TURNS)

            def merge(b, i):
                dve.wait_ge(chunk_used, b.chunks(CPB))
                dve.wait_ge(acc_free[1], b.evacuated_before())
                for t in range(TOK):
                    ins = nc.vector.tensor_tensor(merged[:, t, :], acc[0][t][:, :], gate[:, t, :], ALU.mult)
                ins.then_inc(acc_free[0], 1)
                dve.wait_ge(acc_free[0], b.evacuated())
                for t in range(TOK):
                    ins = nc.vector.tensor_tensor(merged[:, t, :], merged[:, t, :], y[:, t, bass.ds(NB * i, NB)], ALU.add)
                ins.then_inc(merged_ready, 1)

            def split_merged(i):
                for m in range(2):
                    dve.wait_ge(mT_hi_ready, 2 * i + m + 1)
                    ins = nc.vector.tensor_tensor(
                        mT_lo[:, bass.ds(4 * i + 2 * m, 2), :], mis[m].rearrange("p (c s) -> p c s", c=2),
                        mT_hi[:, bass.ds(4 * i + 2 * m, 2), :].bitcast(F32), ALU.subtract)
                ins.then_inc(mT_ready, 1)

            for place in range(4, 12):
                split_at(Blk(B_GR0), place)
            dve.wait_ge(y_scaled, 4 + 1)
            with dve.Fori(0, MERGE_TURNS) as i:
                b = Blk(B_MERGE, 2, i)
                for place in range(4, 20):
                    split_at(b, place)
                    if place == 11:
                        merge(b, i)
                    if place == 14:
                        split_merged(i)

            def add_residual(f):
                b = Blk(B_OUT + f)
                dve.wait_ge(chunk_used, b.chunks(CPB))
                for t in range(TOK):
                    r = res[:, t, f * NB:(f + 1) * NB]
                    nc.vector.tensor_tensor(r, acc[b.parity][t][:, :], r, ALU.add).then_inc(out_ready, 1)

            for place in range(4, CPB * (B_END - B_BR3)):
                split_at(Blk(B_BR3), place)
                if place == 11:
                    merge(Blk(B_BR3), MERGE_TURNS)
                if place == 14:
                    split_merged(MERGE_TURNS)
                if place == 18:
                    dve.wait_ge(res_loaded, 16)
                if place >= 19 and place % CPB == 3:
                    add_residual(place // CPB - 2)
            add_residual(3)

        @block.tensor
        def _(pe):
            def products(b, c, hi, lo):
                pe.wait_ge(lo_ready, b.chunks(c + 1))
                for k in range(KPC):
                    kt = KPC * c + k
                    for t in range(TOK):
                        dst = acc[b.parity][t][:, :]
                        a_hi, a_lo = hi[:, kt, t * P:(t + 1) * P], lo[:, kt, t * P:(t + 1) * P]
                        nc.tensor.matmul(dst, a_hi, w_hi[:, c % RING, k, :], start=(kt == 0), stop=False)
                        nc.tensor.matmul(dst, a_hi, w_lo[:, c % RING, k, :], start=False, stop=False)
                        ins = nc.tensor.matmul(dst, a_lo, w_hi[:, c % RING, k, :], start=False, stop=(kt == KT - 1))
                ins.then_inc(chunk_used, 1)

            def claim(b):
                if b.turn is not None or b.const >= 2:
                    pe.wait_ge(acc_free[b.parity], b.evacuated_before())

            def transposed(dst, src):
                return nc.tensor.transpose(dst, src, ident[:, :])

            def transpose_tiles(src, n, banks):
                for c in range(n):
                    for t in range(TOK):
                        col = (c % 2) * SEQ + t * P
                        ins = transposed(banks[c // 2][:, col:col + P], src[:, t, c * P:(c + 1) * P])
                return ins

            pe.wait_ge(ident_loaded, 16)
            pe.wait_ge(consts_loaded, 16 * N_CONSTS)
            nc.tensor.transpose(mis[3][:, 0:34], vec_rows[:, :], ident[0:34, 0:34]).then_inc(cols_T, 1)

            def transpose_x(g):
                for m in (2 * g, 2 * g + 1):
                    if m == 3:
                        pe.wait_ge(cols_ready, 1)
                    if m >= 4:
                        pe.wait_ge(hT_ready, 2 * (m - 4) + 2)
                    for e in range(2):
                        for t in range(TOK):
                            k = 2 * m + e
                            ins = transposed(mis[m % 4][:, e * SEQ + t * P:e * SEQ + (t + 1) * P],
                                             x_s[:, t, k * P:(k + 1) * P])
                    ins.then_inc(xT_done, 1)

            for g in range(4):
                pe.wait_ge(x_loaded[g], 16)
                transpose_x(g)
                if g >= 1:
                    for c in (2 * g - 2, 2 * g - 1):
                        pe.wait_ge(hT_ready, 2 * c + 2)
                        products(Blk(B_KV), c, hT_hi, hT_lo)
            for c in (6, 7):
                pe.wait_ge(hT_ready, 2 * c + 2)
                products(Blk(B_KV), c, hT_hi, hT_lo)
            with pe.Fori(0, 2) as i:
                for e in range(2):
                    b = Blk(B_Q + e, 2, i)
                    claim(b)
                    for c in range(CPB):
                        products(b, c, hT_hi, hT_lo)

            pe.wait_ge(v_low_loaded, 16)
            with pe.Fori(0, MIX_TURNS) as i:
                for slot in range(MIX_BLOCKS * CPB):
                    b = Blk(B_MIX + slot // CPB, MIX_BLOCKS, i)
                    if slot % CPB == 0:
                        claim(b)
                    products(b, slot % CPB, hT_hi, hT_lo)
                    if slot == 2:
                        pe.wait_ge(qk_staged, i + 1)
                        pe.wait_ge(gT_ready, i + 1)
                        transpose_tiles(qstage, CT, mis)
                        for t in range(TOK):
                            ins = transposed(mis[2][:, t * P:(t + 1) * P], kdup[:, t].rearrange("p e d -> p (e d)"))
                        ins.then_inc(qkT_done, 1)
                    if slot % 2 == 0 and 0 <= (slot - 4) // 2 < GROUP:
                        h = (slot - 4) // 2
                        if h == 0:
                            pe.wait_ge(qkT_ready, i + 1)
                        else:
                            pe.wait_ge(neg_max_ready, GROUP * i + h)
                        r = HD * (h % 2)
                        nc.tensor.matmul(mis[0][:, 0:128], qT[r:r + HD, h // 2, 0:P], kT[r:r + HD, 0:P],
                                         start=True, stop=True)
                        nc.tensor.matmul(mis[0][:, 128:320], qT[r:r + HD, h // 2, P:SEQ], kT[r:r + HD, CHUNK:SEQ],
                                         start=True, stop=True).then_inc(scores_done, 1)
                    if slot % 2 == 1 and 0 <= (slot - 7) // 2 < GROUP:
                        h = (slot - 7) // 2
                        pe.wait_ge(probs_ready, GROUP * i + h + 1)
                        if h > 0:
                            pe.wait_ge(pT_ready, GROUP * i + h)
                        transposed(mis[1][:, 0:128], probs[:, h % 2, 0:128])
                        transposed(mis[1][:, 128:256], probs[:, h % 2, 192:320])
                        transposed(mis[1][0:HD, 256:384], probs[:, h % 2, 128:192]).then_inc(pT_done, 1)
                    if slot % 2 == 1 and 0 <= (slot - 9) // 2 < GROUP:
                        h = (slot - 9) // 2
                        pe.wait_ge(pT_ready, GROUP * i + h + 1)
                        v = bass.ds(HD * i + KVW, HD)
                        hc = slice(h * HD, (h + 1) * HD)
                        nc.tensor.matmul(mis[2][:, hc], pT[:, h % 2, 0:128], kv[:, 0, v], start=True, stop=True)
                        nc.tensor.matmul(mis[3][:, hc], pT[:, h % 2, 128:256], kv[:, 1, v], start=True, stop=False)
                        ins = nc.tensor.matmul(mis[3][:, hc], pT[0:HD, h % 2, 256:384], v_low[:, bass.ds(HD * i, HD)],
                                               start=False, stop=True)
                        if h == GROUP - 1:
                            ins.then_inc(pv_done, 1)
                    if slot == 25:
                        pe.wait_ge(acc_free[1], Blk(B_MIX, MIX_BLOCKS, i).evacuated())
                        transpose_tiles(rqk_stage, CT, mis).then_inc(rqkT_done, 1)
                    if slot == 26:
                        pe.wait_ge(gated_ready, i + 1)
                        transpose_tiles(gate, CT, mis[2:4]).then_inc(gT_done, 1)

            pe.wait_ge(gT_ready, MIX_TURNS + 1)
            with pe.Fori(0, 2) as i:
                for e in range(2):
                    b = Blk(B_BRA + e, 2, i)
                    claim(b)
                    for c in range(CPB):
                        products(b, c, gT_hi, gT_lo)

            with pe.Fori(0, RET_TURNS) as j:
                for slot in range(2 * CPB):
                    b = Blk(B_GA + slot // CPB, 2, j)
                    if slot % CPB == 0:
                        claim(b)
                    products(b, slot % CPB, hT_hi, hT_lo)
                    if slot % 2 == 0 and 0 <= (slot - 2) // 2 < RET_PER:
                        n = (slot - 2) // 2
                        if n == 0:
                            pe.wait_ge(keys_copied, j + 1)
                            pe.wait_ge(gT_ready, j + (MIX_TURNS + 1))
                        else:
                            pe.wait_ge(ret_weighted, RET_PER * j + n)
                        rq = rqkT[:, bass.ds(RET_PER * j + n, 1), :].rearrange("p a s -> p (a s)")
                        nc.tensor.matmul(mis[0][:, 0:SEQ], kstage[:, n, 0:P], rq, start=True, stop=True)
                        nc.tensor.matmul(mis[0][:, SEQ:SEQ + P], kstage[:, n, P:SEQ], rq[:, P:SEQ],
                                         start=True, stop=True).then_inc(ret_scores, 1)
                    if slot % 2 == 0 and 0 <= (slot - 4) // 2 < RET_PER:
                        n = (slot - 4) // 2
                        pe.wait_ge(ret_weighted, RET_PER * j + n + 1)
                        if n >= 2:
                            pe.wait_ge(ret_centred, RET_PER * j + n - 1)
                        o_ps = mis[2 + n % 2]
                        v = bass.ds(RET_PER * RET_V * j + RET_V * n, RET_V)
                        nc.tensor.matmul(o_ps[:, 0:RET_V], ret_w[:, n % 2, 0:P], rv[:, 0, v], start=True, stop=True)
                        nc.tensor.matmul(o_ps[:, RET_V:2 * RET_V], ret_w[:, n % 2, P:2 * P], rv[:, 0, v],
                                         start=True, stop=False)
                        nc.tensor.matmul(o_ps[:, RET_V:2 * RET_V], ret_w[:, n % 2, 2 * P:3 * P], rv[:, 1, v],
                                         start=False, stop=True).then_inc(ret_done, 1)
                    if slot == 15:
                        pe.wait_ge(ret_staged, j + 1)
                        transpose_tiles(ret_gated, 8, mis).then_inc(retT_done, 1)

            def transpose_merged(i):
                pe.wait_ge(merged_ready, i + 1)
                transpose_tiles(merged, CT, mis).then_inc(mT_done, 1)

            claim(Blk(B_GR0))
            for c in range(CPB):
                products(Blk(B_GR0), c, hT_hi, hT_lo)
            pe.wait_ge(gT_ready, MIX_TURNS + RET_TURNS + 1)
            with pe.Fori(0, MERGE_TURNS) as i:
                for slot in range(2 * CPB):
                    b = Blk(B_MERGE + slot // CPB, 2, i)
                    if slot % CPB == 0:
                        claim(b)
                    if slot < CPB:
                        products(b, slot, gT_hi, gT_lo)
                    else:
                        products(b, slot % CPB, hT_hi, hT_lo)
                    if slot == 10:
                        transpose_merged(i)
            claim(Blk(B_BR3))
            for c in range(CPB):
                products(Blk(B_BR3), c, gT_hi, gT_lo)

            for f in range(4):
                if f < 2:
                    claim(Blk(B_OUT + f))
                else:
                    pe.wait_ge(out_ready, TOK * (f - 1))
                for c in range(CPB):
                    if f == 0 and c % 2 == 0:
                        pe.wait_ge(mT_ready, c // 2 + 1)
                    products(Blk(B_OUT + f), c, mT_hi, mT_lo)
                    if f == 0 and c == 2:
                        transpose_merged(MERGE_TURNS)


def shape_constants():
    import numpy as np

    tok = np.arange(P)
    masked = np.float32(1e34)
    q0, k0 = tok[:, None], tok[None, :]
    d0 = np.where(k0 // CHUNK <= q0 // CHUNK, np.abs(q0 - k0), masked)
    q1, k1 = P + tok[:, None], np.arange(CHUNK, SEQ)[None, :]
    near = (k1 // CHUNK <= q1 // CHUNK) & (k1 // CHUNK >= q1 // CHUNK - 1)
    d1 = np.where(near, np.abs(q1 - k1), masked)
    distance = np.concatenate([d0, d1], axis=1).astype(np.float32)
    neg_slopes = -np.exp2(-8.0 * np.arange(1, HEADS + 1, dtype=np.float64) / HEADS).astype(np.float32)[None, :]
    log_g = np.log(1.0 - np.exp2(-5.0 - np.arange(RET_HEADS, dtype=np.float64)))
    keys, queries = tok[:, None], np.arange(SEQ)[None, :]
    seen = keys // CHUNK <= queries // CHUNK
    decay = np.exp(np.abs(queries - keys)[:, None, :] * log_g[None, :, None]) * seen[:, None, :] * RET_QK ** -0.5
    return {"identity": np.eye(P, dtype=np.float32), "distance": distance, "neg_slopes": neg_slopes,
            "decay": decay.astype(np.float32)}


_INS = ["x", "norm_w", "w_in", "q_norm_w", "k_norm_w", "sinks", "ret_gn_w", "w_br_attn", "w_br_ret", "w_out"]


def kernel(**inputs):
    import numpy as np
    import concourse.bacc as bacc
    from concourse.bass_utils import run_bass_kernel_spmd

    nc = bacc.Bacc("TRN2", target_bir_lowering=False, num_devices=1)
    arrays, args = {}, []
    for name, a in [(n, inputs[n]) for n in _INS] + list(shape_constants().items()):
        a = np.ascontiguousarray(a)
        arrays[f"in_{name}"] = a
        args.append(nc.dram_tensor(f"in_{name}", a.shape, mybir.dt.from_np(a.dtype), kind="ExternalInput").ap())
    args.append(nc.dram_tensor("out_x", (1, SEQ, D), F32, kind="ExternalOutput").ap())
    hybrid_block_kernel(nc, *args)
    r = run_bass_kernel_spmd(nc, [arrays], core_ids=[0])
    return r.results[0]["out_x"]
```
